# Optimizing a Trainium2 kernel written in Bass

```python
import math
import jax, jax.numpy as jnp
from jax import lax
import numpy as np

D_MODEL = 1024
BATCH = 1
SEQ = 512
DEPTH = 1

D_FF = 2816
D_MIX = D_MODEL
A_WIDTH = D_MIX // 2
A_HEADS = 8
A_HEAD_DIM = A_WIDTH // A_HEADS
CHUNK = 128
B_WIDTH = D_MIX - A_WIDTH
POOL_WINDOWS = (2, 4, 8, 16)
B_GROUPS = len(POOL_WINDOWS)
B_GROUP_DIM = B_WIDTH // B_GROUPS
IN_COLS = 2 * A_WIDTH + B_WIDTH
EPS = 1e-6

kernel_name = "hybrid_gmlp_pool_macaron_block"

def rmsnorm(x, g):
    xf = x.astype(jnp.float32)
    r = lax.rsqrt(jnp.mean(xf * xf, axis=-1, keepdims=True) + EPS)
    return (xf * r).astype(x.dtype) * g

def swiglu(h, w_gate, w_up, w_down):
    return (jax.nn.silu(h @ w_gate) * (h @ w_up)) @ w_down

def gmlp_mixer(u, v, v_gain, w_s, b_s):
    bsz, seq, _ = u.shape
    u = jax.nn.gelu(u)
    v = jax.nn.gelu(v).reshape(bsz, seq, A_HEADS, A_HEAD_DIM)
    v = rmsnorm(v, v_gain.reshape(A_HEADS, A_HEAD_DIM))
    v = v.reshape(bsz, seq // CHUNK, CHUNK, A_HEADS, A_HEAD_DIM)
    causal = jnp.tril(jnp.ones((CHUNK, CHUNK), dtype=bool))
    w = jnp.where(causal[None], w_s, jnp.zeros_like(w_s))
    v = jnp.einsum('hts,bnshd->bnthd', w, v) + b_s.T[None, None, :, :, None]
    return u * v.reshape(bsz, seq, A_WIDTH)

def pool_mixer(z, w_pool, scale):
    bsz, seq, _ = z.shape
    zf = z.astype(jnp.float32)
    cs = jnp.concatenate([jnp.zeros((bsz, 1, B_WIDTH), jnp.float32),
                          jnp.cumsum(zf, axis=1)], axis=1)
    pos = jnp.arange(1, seq + 1, dtype=jnp.int32)
    outs = []
    for g, win in enumerate(POOL_WINDOWS):
        sl = slice(g * B_GROUP_DIM, (g + 1) * B_GROUP_DIM)
        c = cs[..., sl]
        upper = c[:, 1:]
        lower = jnp.concatenate([jnp.zeros((bsz, win - 1, B_GROUP_DIM), jnp.float32),
                                 c[:, :seq - win + 1]], axis=1)
        count = jnp.minimum(pos, win).astype(jnp.float32)[None, :, None]
        d = ((upper - lower) / count - zf[..., sl]).astype(z.dtype)
        outs.append(d @ w_pool[g])
    return jnp.concatenate(outs, axis=-1) * scale

def setup_inputs(seed: int = 0) -> dict:
    key = jax.random.key(seed)
    ks = jax.random.split(key, 20)
    f32 = jnp.float32
    L = DEPTH

    def nrm(k, shape, s):
        return jax.random.normal(k, shape, f32) * s

    def gain(k, shape):
        return 1.0 + 0.05 * jax.random.normal(k, shape, f32)

    return {
        "x": jax.random.normal(ks[0], (BATCH, SEQ, D_MODEL), f32),
        "ffn1_norm": gain(ks[1], (L, D_MODEL)),
        "ffn1_w_gate": nrm(ks[2], (L, D_MODEL, D_FF), D_MODEL ** -0.5),
        "ffn1_w_up": nrm(ks[3], (L, D_MODEL, D_FF), D_MODEL ** -0.5),
        "ffn1_w_down": nrm(ks[4], (L, D_FF, D_MODEL), D_FF ** -0.5),
        "mix_norm": gain(ks[5], (L, D_MODEL)),
        "w_in": nrm(ks[6], (L, D_MODEL, IN_COLS), D_MODEL ** -0.5),
        "gmlp_v_norm": gain(ks[7], (L, A_WIDTH)),
        "gmlp_w_s": nrm(ks[8], (L, A_HEADS, CHUNK, CHUNK), 0.5 * CHUNK ** -0.5),
        "gmlp_b_s": 1.0 + 0.1 * jax.random.normal(ks[9], (L, A_HEADS, CHUNK), f32),
        "pool_w": nrm(ks[10], (L, B_GROUPS, B_GROUP_DIM, B_GROUP_DIM), B_GROUP_DIM ** -0.5),
        "pool_scale": gain(ks[11], (L, B_WIDTH)),
        "w_out": nrm(ks[12], (L, D_MIX, D_MODEL), D_MIX ** -0.5),
        "ffn2_norm": gain(ks[13], (L, D_MODEL)),
        "ffn2_w_gate": nrm(ks[14], (L, D_MODEL, D_FF), D_MODEL ** -0.5),
        "ffn2_w_up": nrm(ks[15], (L, D_MODEL, D_FF), D_MODEL ** -0.5),
        "ffn2_w_down": nrm(ks[16], (L, D_FF, D_MODEL), D_FF ** -0.5),
        "final_norm": gain(ks[17], (D_MODEL,)),
    }

def reference(x, ffn1_norm, ffn1_w_gate, ffn1_w_up, ffn1_w_down, mix_norm, w_in,
              gmlp_v_norm, gmlp_w_s, gmlp_b_s, pool_w, pool_scale, w_out,
              ffn2_norm, ffn2_w_gate, ffn2_w_up, ffn2_w_down, final_norm):
    for l in range(DEPTH):
        x = x + 0.5 * swiglu(rmsnorm(x, ffn1_norm[l]), ffn1_w_gate[l], ffn1_w_up[l], ffn1_w_down[l])
        p = rmsnorm(x, mix_norm[l]) @ w_in[l]
        u_a = p[..., :A_WIDTH]
        v_a = p[..., A_WIDTH:2 * A_WIDTH]
        z_b = p[..., 2 * A_WIDTH:]
        y_a = gmlp_mixer(u_a, v_a, gmlp_v_norm[l], gmlp_w_s[l], gmlp_b_s[l])
        y_b = pool_mixer(z_b, pool_w[l], pool_scale[l])
        x = x + jnp.concatenate([y_a, y_b], axis=-1) @ w_out[l]
        x = x + 0.5 * swiglu(rmsnorm(x, ffn2_norm[l]), ffn2_w_gate[l], ffn2_w_up[l], ffn2_w_down[l])
    return rmsnorm(x, final_norm)


_drawn_inputs = setup_inputs


def setup_inputs(seed=0):
    import zlib

    import numpy as np

    out = dict(_drawn_inputs(seed))
    spreads = {}
    factors = {'gmlp_v_norm': 8.0, 'ffn2_norm': 3.405}
    for name, (base, spread) in spreads.items():
        noise = np.random.default_rng([zlib.crc32(name.encode()), seed]).standard_normal(out[name].shape)
        drawn = base * np.exp(spread * noise) if base else spread * noise
        out[name] = __import__('jax').numpy.asarray(drawn.astype(out[name].dtype))
    for name, factor in factors.items():
        out[name] = (out[name] * factor).astype(out[name].dtype)
    return out
```

```python
from contextlib import ExitStack

import concourse.bass as bass
from concourse import mybir

F32 = mybir.dt.float32
F32R = mybir.dt.float32r
ALU = mybir.AluOpType
ACT = mybir.ActivationFunctionType
AX_X = mybir.AxisListType.X

P = 128
D_MODEL = 1024
SEQ = 512
D_FF = 2816
A_WIDTH = 512
A_HEADS = 8
HEAD_DIM = A_WIDTH // A_HEADS
POOL_WINDOWS = (2, 4, 8, 16)
EPS = 1e-6
GELU_CUBIC = 0.044715
GELU_SLOPE = 2.0 * (2.0 / 3.141592653589793) ** 0.5

KD = D_MODEL // P
KF = D_FF // P
TT = SEQ // P
HALF = KD // 2
GRAIN = 8 * P
SLOTS = 4
PAIR = 2
PAD = 16

QUAD_F = KF // PAIR
QUAD_M = KD // PAIR
GATE_UP = 2 * KF
FFN_GRAINS = GATE_UP + 2 * QUAD_F
MIX_Z, MIX_V, MIX_P, MIX_U, MIX_S, MIX_U3, MIX_OUT = 0, 4, 8, 9, 12, 13, 14
MIX_GRAINS = MIX_OUT + 2 * QUAD_M


def plan_stream():
    slot_of, pair_of, pairs = [], [], []
    slot = 0
    for n, runs in ((0, (GATE_UP, QUAD_F, QUAD_F)), (1, (MIX_GRAINS,)), (2, (GATE_UP, QUAD_F, QUAD_F))):
        for run in runs:
            for g in range(0, run, PAIR):
                k = min(PAIR, run - g)
                pairs.append((len(slot_of), k))
                for j in range(k):
                    slot_of.append((slot + j) % SLOTS)
                    pair_of.append((len(pairs) - 1, j))
                slot = (slot + PAIR) % SLOTS
    return slot_of, pair_of, pairs


SLOT_OF, PAIR_OF, PAIRS = plan_stream()
N_GRAINS = len(SLOT_OF)
FFN_GRAIN = (0, FFN_GRAINS + MIX_GRAINS)
MIX_GRAIN = FFN_GRAINS


def same_slot_before(n):
    return next((m for m in range(n - 1, -1, -1) if SLOT_OF[m] == SLOT_OF[n]), None)


def build_block(nc: bass.Bass, x_t, stream, columns, spatial_bias, out_t):
    with ExitStack() as ctx:
        def sb(name, shape, dt=F32):
            return ctx.enter_context(nc.sbuf_tensor(name, shape, dt))

        def sem(name):
            return ctx.enter_context(nc.semaphore(name))

        x_res = sb("x_res", [P, KD, SEQ])
        x_hi = sb("x_hi", [P, KD, SEQ], F32R)
        x_lo = sb("x_lo", [P, KD, SEQ], F32R)
        h_hi = sb("h_hi", [P, KF, SEQ], F32R)
        h_lo = sb("h_lo", [P, KF, SEQ], F32R)
        DIFF, VPAD = KD, KD + TT
        w_raw = sb("w_raw", [P, SLOTS, GRAIN])
        w_hi = sb("w_hi", [P, SLOTS, GRAIN], F32R)
        w_lo = sb("w_lo", [P, SLOTS, GRAIN], F32R)
        tile_g = sb("tile_g", [P, 2, PAD + SEQ])
        tile_s = sb("tile_s", [P, 2, PAD + SEQ])
        tile_u = sb("tile_u", [P, 2, PAD + SEQ])
        square_sum = sb("square_sum", [P, SEQ])
        r_row = sb("r_row", [P, SEQ])
        r_col = sb("r_col", [P, TT])
        mean_col = sb("mean_col", [P, TT])
        v_sums = sb("v_sums", [P, 2, A_HEADS])
        v_scale = sb("v_scale", [P, 2, A_HEADS])
        minus_half = sb("minus_half", [P, A_HEADS])
        ident = sb("ident", [P, P])
        ones = sb("ones", [P, P])
        inv_count = sb("inv_count", [P, PAD])
        bias_bc = sb("bias_bc", [P, A_HEADS // 2, P])
        cols = sb("cols", [P, 4 * KD + 8])
        GAIN_MIX, GAIN_FINAL, GAIN_V, POOL_SCALE = 2 * KD, 3 * KD, 4 * KD, 4 * KD + 4
        GAIN_FFN = (0, KD)

        ps = ctx.enter_context(nc.psum_tensor("ps", [P, 8, SEQ], F32))
        R_BANK, COL_BANK = 4, 5

        x_loaded = [sem(f"x_loaded{c}") for c in range(KD)]
        consts_loaded = sem("consts_loaded")
        pads_set = sem("pads_set")
        consts_set = sem("consts_set")
        ranks_set = sem("ranks_set")
        inv_set = sem("inv_set")
        weights_loaded = [sem(f"weights_loaded{h}") for h in range(2)]
        masked = sem("masked")
        whi_ready = sem("whi_ready")
        wlo_ready = sem("wlo_ready")
        w_used = sem("w_used")
        gate_ready = sem("gate_ready")
        up_ready = sem("up_ready")
        sig_ready = sem("sig_ready")
        silu_ready = sem("silu_ready")
        hid_ready = sem("hid_ready")
        hhi_ready = sem("hhi_ready")
        hlo_ready = sem("hlo_ready")
        chunk_done = sem("chunk_done")
        xnew_ready = sem("xnew_ready")
        xhi_ready = sem("xhi_ready")
        xlo_ready = sem("xlo_ready")
        square_ready = sem("square_ready")
        squares_added = sem("squares_added")
        colsum_done = sem("colsum_done")
        mean_ready = sem("mean_ready")
        rcol_ready = sem("rcol_ready")
        diag_ready = sem("diag_ready")
        rowsum_done = sem("rowsum_done")
        rrow_ready = sem("rrow_ready")
        p_done = sem("p_done")
        s_done = sem("s_done")
        z_ready = sem("z_ready")
        windows_ready = sem("windows_ready")
        pool_step = sem("pool_step")
        head_fixed = sem("head_fixed")
        diff_ready = sem("diff_ready")
        dhi_ready = sem("dhi_ready")
        dlo_ready = sem("dlo_ready")
        yhi_ready = sem("yhi_ready")
        ylo_ready = sem("ylo_ready")
        vzero_set = sem("vzero_set")
        arg_ready = sem("arg_ready")
        argsq_ready = sem("argsq_ready")
        cubic_ready = sem("cubic_ready")
        gsig_ready = sem("gsig_ready")
        gelu_ready = sem("gelu_ready")
        vsquare_ready = sem("vsquare_ready")
        vsum_ready = sem("vsum_ready")
        vmean_ready = sem("vmean_ready")
        vscale_ready = sem("vscale_ready")
        vnorm_ready = sem("vnorm_ready")
        vhi_ready = sem("vhi_ready")
        vlo_ready = sem("vlo_ready")
        spat_ready = sem("spat_ready")
        ya_ready = sem("ya_ready")
        out_ready = sem("out_ready")
        out_stored = sem("out_stored")

        def body(tile, b):
            return tile[:, b, PAD:PAD + SEQ]

        def v_block(h, n, head):
            return h[:, VPAD + 2 * n + head // 4, (head % 4) * P:(head % 4 + 1) * P]

        def v_halves(h, n, half):
            two = h[:, VPAD + 2 * n:VPAD + 2 * n + 2, :].rearrange("p a (b c) -> p (a b) c", b=4)
            two = two.rearrange("p (q e) c -> p q e c", e=2)
            return two[:, :, half, half * HEAD_DIM:(half + 1) * HEAD_DIM]

        def ffn_count(f):
            return KF * f, 2 * KD * f, 2 * f

        block = ctx.enter_context(nc.Block())

        @block.sync
        def _(sp):
            def load_pair(p):
                first, k = PAIRS[p]
                before = [same_slot_before(first + j) for j in range(k)]
                if before[0] is not None:
                    sp.wait_ge(wlo_ready, max(before) + 1)
                s = SLOT_OF[first]
                sp.dma_start(w_raw[:, s:s + k, :], stream[p, :, 0:k * GRAIN]).then_inc(
                    weights_loaded[p % 2], 16)

            p = 0
            for f in range(2):
                g0 = FFN_GRAIN[f]
                p0 = PAIR_OF[g0][0]
                for p in range(p0, p0 + 2):
                    load_pair(p)
                with sp.Fori(1, KF // 2) as i:
                    for u in range(2):
                        s = SLOT_OF[g0 + PAIR * u]
                        sp.wait_ge(wlo_ready, g0 + PAIR * u - 2 + SLOTS * i)
                        sp.dma_start(w_raw[:, s:s + PAIR, :], stream[p0 + u + 2 * i, :, :]).then_inc(
                            weights_loaded[(p0 + u) % 2], 16)
                end = PAIR_OF[FFN_GRAIN[1]][0] if f == 0 else len(PAIRS)
                for p in range(p0 + KF, end):
                    load_pair(p)
            for c in range(KD):
                sp.wait_ge(out_ready, c + 1)
                sp.dma_start(out_t[c], x_res[:, c, :]).then_inc(out_stored, 16)
            sp.wait_ge(out_stored, 16 * KD)

        @block.tensor
        def _(pe):
            def product(out, stat, mov, start, stop):
                (s_hi, s_lo), (m_hi, m_lo) = stat, mov
                nc.tensor.matmul(out, s_hi, m_hi, start=start, stop=False)
                nc.tensor.matmul(out, s_hi, m_lo, start=False, stop=False)
                return nc.tensor.matmul(out, s_lo, m_hi, start=False, stop=stop)

            def weights(slot, a, n=P):
                return w_hi[:, slot, a:a + n], w_lo[:, slot, a:a + n]

            def chunk(pair, k, a=0, n=SEQ):
                return pair[0][:, k, a:a + n], pair[1][:, k, a:a + n]

            XS, HS = (x_hi, x_lo), (h_hi, h_lo)

            def unit(slot, bank, fresh=None):
                for half in range(2):
                    for w in range(2):
                        for k in range(half * HALF, (half + 1) * HALF):
                            if fresh is not None and w == 0:
                                pe.wait_ge(xlo_ready, fresh + k + 1)
                            last = product(ps[:, bank + w, :], weights(slot[w], k * P), chunk(XS, k),
                                           k == 0, k == KD - 1)
                        if half:
                            last.then_inc(w_used, 1)

            def column_sums(norm):
                pe.wait_ge(consts_set, 1)
                pe.wait_ge(squares_added, KD * (norm + 1))
                for t in range(TT):
                    last = nc.tensor.matmul(ps[:, COL_BANK, t:t + 1], square_sum[:, t * P:(t + 1) * P],
                                            ones[:, 0:1], start=True, stop=True)
                last.then_inc(colsum_done, 1)

            def row_scale(norm):
                pe.wait_ge(diag_ready, norm + 1)
                nc.tensor.matmul(ps[:, R_BANK, :], ones[:, :], body(tile_u, 0),
                                 start=True, stop=True).then_inc(rowsum_done, 1)

            def gate_up(f):
                g0 = FFN_GRAIN[f]
                u0, c0, norm = ffn_count(f)
                slots = [(SLOT_OF[g0 + 2 * u], SLOT_OF[g0 + 2 * u + 1]) for u in range(2)]
                for u in range(2):
                    pe.wait_ge(wlo_ready, g0 + 2 * u + 2)
                    unit(slots[u], 2 * u, c0 if u == 0 else None)
                    if u == 0:
                        column_sums(norm)
                row_scale(norm)
                with pe.Fori(1, KF // 2) as i:
                    for u in range(2):
                        pe.wait_ge(wlo_ready, g0 + 2 * u + 2 + SLOTS * i)
                        pe.wait_ge(up_ready, u0 + u - 1 + 2 * i)
                        unit(slots[u], 2 * u)

            def quad_granule(slot, bank, ks, first, last_one):
                for m in range(HALF):
                    for j, k in enumerate(ks):
                        last = product(ps[:, bank(m), :], weights(slot, j * HALF * P + m * P), chunk(HS, k),
                                       first and j == 0, last_one and j == 1)
                    if last_one and m < HALF - 1:
                        last.then_inc(chunk_done, 1)
                return last

            def down(f):
                g0 = FFN_GRAIN[f] + GATE_UP
                u0, _, _ = ffn_count(f)
                for q in range(2):
                    bank0 = 4 * (1 - q)
                    for g in range(QUAD_F):
                        n = g0 + QUAD_F * q + g
                        pe.wait_ge(wlo_ready, n + 1)
                        if q == 0:
                            pe.wait_ge(hlo_ready, u0 + 2 * g + 2)
                        last = quad_granule(SLOT_OF[n], lambda m: bank0 + m, (2 * g, 2 * g + 1),
                                            g == 0, g == QUAD_F - 1)
                        last.then_inc(w_used, 1)

            def mixer():
                g0 = MIX_GRAIN

                def tile_of(n, bank, fresh):
                    pe.wait_ge(wlo_ready, g0 + n + 1)
                    for k in range(KD):
                        if fresh:
                            pe.wait_ge(xlo_ready, KD + k + 1)
                        last = product(ps[:, bank, :], weights(SLOT_OF[g0 + n], k * P), chunk(XS, k),
                                       k == 0, k == KD - 1)
                    last.then_inc(w_used, 1)

                for i in range(4):
                    pe.wait_ge(xnew_ready, HALF + i + 1)
                    tile_of(MIX_Z + i, i, i == 0)
                    if i == 0:
                        column_sums(1)
                    if i == 1:
                        row_scale(1)
                pe.wait_ge(rrow_ready, 2)
                for g in range(4):
                    pe.wait_ge(wlo_ready, g0 + MIX_V + g + 1)
                    for t in range(TT):
                        for j in range(2):
                            k = 2 * g + j
                            last = product(ps[:, 4 + t, :], chunk(XS, k, t * P, P),
                                           weights(SLOT_OF[g0 + MIX_V + g], j * SEQ, SEQ),
                                           k == 0, k == KD - 1)
                    last.then_inc(w_used, 1)
                pe.wait_ge(wlo_ready, g0 + MIX_P + 1)
                for g in range(4):
                    pe.wait_ge(dlo_ready, g + 1)
                    last = product(ps[:, g, :], weights(SLOT_OF[g0 + MIX_P], g * P), chunk(HS, DIFF + g),
                                   True, True)
                    last.then_inc(p_done if g < 3 else w_used, 1)
                for i in range(3):
                    pe.wait_ge(ylo_ready, i + 1)
                    tile_of(MIX_U + i, i, False)
                pe.wait_ge(wlo_ready, g0 + MIX_S + 1)
                pe.wait_ge(vlo_ready, 2 * TT)
                for q in range(A_HEADS // 2):
                    for n in range(TT):
                        for e in range(2):
                            head = 2 * q + e
                            last = product(ps[:, 4 + q, n * P:(n + 1) * P],
                                           (v_block(h_hi, n, head), v_block(h_lo, n, head)),
                                           weights(SLOT_OF[g0 + MIX_S], head * P), e == 0, e == 1)
                    last.then_inc(s_done if q < 3 else w_used, 1)
                pe.wait_ge(ylo_ready, 4)
                tile_of(MIX_U3, 3, False)
                for q in range(2):
                    for g, (ks, need) in enumerate((((4, 5), 4), ((6, 7), 4), ((0, 1), 6), ((2, 3), 8))):
                        n = g0 + MIX_OUT + QUAD_M * q + g
                        pe.wait_ge(wlo_ready, n + 1)
                        if q == 0:
                            pe.wait_ge(ylo_ready, need)
                        for m in range(HALF):
                            if g == 0 and q == 0:
                                pe.wait_ge(arg_ready, TT + m + 1)
                            if g == 0 and q == 1:
                                pe.wait_ge(spat_ready, m + 1)
                            for j, k in enumerate(ks):
                                last = product(ps[:, 4 * q + m, :],
                                               weights(SLOT_OF[n], j * HALF * P + m * P), chunk(HS, k),
                                               g == 0 and j == 0, g == QUAD_M - 1 and j == 1)
                            if g == QUAD_M - 1 and m < HALF - 1:
                                last.then_inc(chunk_done, 1)
                        last.then_inc(w_used, 1)

            gate_up(0)
            down(0)
            mixer()
            gate_up(1)
            down(1)
            column_sums(3)
            row_scale(3)

        @block.scalar
        def _(act):
            def copy(out, in_, scale=1.0):
                return nc.scalar.activation(out, in_, ACT.Copy, scale=scale)

            def split_hi(n):
                p, j = PAIR_OF[n]
                act.wait_ge(weights_loaded[p % 2], 16 * (p // 2 + 1))
                if (m := same_slot_before(n)) is not None:
                    act.wait_ge(w_used, m + 1)
                if n == MIX_GRAIN + MIX_S:
                    act.wait_ge(masked, 1)
                cut = TT * P if n == MIX_GRAIN + MIX_P else GRAIN
                copy(w_hi[:, SLOT_OF[n], 0:cut], w_raw[:, SLOT_OF[n], 0:cut]).then_inc(whi_ready, 1)

            def chunk_parts(c, count, gain, has_hi=True):
                if has_hi:
                    nc.scalar.activation(x_hi[:, c, :], x_res[:, c, :], ACT.Copy,
                                         scale=cols[:, gain + c:gain + c + 1]).then_inc(xhi_ready, 1)
                if c == 0:
                    nc.scalar.activation(square_sum[:, :], x_res[:, c, :], ACT.Square).then_inc(square_ready, 1)
                else:
                    act.wait_ge(squares_added, count + c - 1)
                    nc.scalar.activation(body(tile_s, c % 2), x_res[:, c, :],
                                         ACT.Square).then_inc(square_ready, 1)

            def copy_r(norm):
                act.wait_ge(rowsum_done, norm + 1)
                copy(r_row[:, :], ps[:, R_BANK, :]).then_inc(rrow_ready, 1)

            def sigmoid_gate(j, b):
                act.wait_ge(gate_ready, j + 1)
                nc.scalar.activation(body(tile_s, b), body(tile_g, b), ACT.Sigmoid).then_inc(sig_ready, 1)

            def hidden_hi(j, b, at):
                act.wait_ge(hid_ready, j + 1)
                copy(h_hi[:, at, :], body(tile_u, b)).then_inc(hhi_ready, 1)

            def gate_up(f):
                g0 = FFN_GRAIN[f]
                u0, _, norm = ffn_count(f)
                copy_r(norm)
                for j in range(2):
                    sigmoid_gate(u0 + j, j)
                    split_hi(g0 + 4 + 2 * j)
                    hidden_hi(u0 + j, j, j)
                    split_hi(g0 + 5 + 2 * j)
                last = KF // 2 - 1
                p0 = PAIR_OF[g0][0]

                def split_ahead(i, c):
                    p = p0 + c // 2
                    act.wait_ge(weights_loaded[p % 2], 16 * (p // 2 + 2) + 16 * i)
                    act.wait_ge(w_used, g0 + c + 1 + SLOTS * i)
                    s = SLOT_OF[g0 + c]
                    copy(w_hi[:, s, :], w_raw[:, s, :]).then_inc(whi_ready, 1)

                with act.Fori(1, last) as i:
                    for j in range(2):
                        sigmoid_gate(u0 + j + 2 * i, j)
                        split_ahead(i, 2 * j)
                        hidden_hi(u0 + j + 2 * i, j, j + 2 * i)
                        split_ahead(i, 2 * j + 1)
                for j in range(2 * last, KF):
                    sigmoid_gate(u0 + j, j % 2)
                    split_hi(g0 + 4 + 2 * j)
                    hidden_hi(u0 + j, j % 2, j)
                    split_hi(g0 + 5 + 2 * j)

            def projection(n0, quad, c0, count, gain, has_hi=True):
                for step in range(2 * quad):
                    q, g = divmod(step, quad)
                    if step == 2 * quad - 1:
                        for c in range(HALF, KD):
                            act.wait_ge(xnew_ready, c0 + c + 1)
                            chunk_parts(c, count, gain, has_hi)
                    if q == 1 and g < HALF and step != 2 * quad - 1:
                        act.wait_ge(xnew_ready, c0 + g + 1)
                        chunk_parts(g, count, gain, has_hi)
                    if q == 1 and quad == HALF and step == 2 * quad - 2:
                        act.wait_ge(xnew_ready, c0 + g + 2)
                        chunk_parts(g + 1, count, gain, has_hi)
                    if n0 + step + SLOTS < N_GRAINS:
                        split_hi(n0 + step + SLOTS)

            for c in range(KD):
                act.dma_start(x_res[:, c, :], x_t[c]).then_inc(x_loaded[c], 16)
                if c == 0:
                    act.dma_start(cols[:, :], columns).then_inc(consts_loaded, 16)
            for e in range(2):
                act.dma_start(bias_bc[e * HEAD_DIM:(e + 1) * HEAD_DIM, :, :],
                              spatial_bias[e:e + 1, :, :].to_broadcast([HEAD_DIM, A_HEADS // 2, P])
                              ).then_inc(consts_loaded, 16)
            act.wait_ge(consts_loaded, 48)
            for c in range(KD):
                act.wait_ge(x_loaded[c], 16)
                chunk_parts(c, 0, GAIN_FFN[0])
                if c in (1, 3):
                    split_hi(c - 1)
                    split_hi(c)
            gate_up(0)
            projection(GATE_UP, QUAD_F, 0, KD, GAIN_MIX)

            g0 = MIX_GRAIN
            for i in range(4):
                split_hi(g0 + 4 + i)
                if i == 1:
                    copy_r(1)
            for g in range(4):
                act.wait_ge(diff_ready, g + 1)
                copy(h_hi[:, DIFF + g, :], body(tile_s, g % 2)).then_inc(dhi_ready, 1)
            for i in range(3):
                split_hi(g0 + 8 + i)

            def gelu_square(e):
                act.wait_ge(arg_ready, e + 1)
                nc.scalar.activation(body(tile_s, e % 2), body(tile_g, e % 2), ACT.Square,
                                     scale=GELU_CUBIC ** 0.5).then_inc(argsq_ready, 1)

            def gelu_sigmoid(e):
                act.wait_ge(cubic_ready, e + 1)
                nc.scalar.activation(body(tile_s, e % 2), body(tile_s, e % 2), ACT.Sigmoid,
                                     scale=GELU_SLOPE).then_inc(gsig_ready, 1)

            split_at = iter((11, 12, 13, 14, 15, 16, 17))
            for pair in range(2):
                es = (2 * pair, 2 * pair + 1)
                for e in es:
                    gelu_square(e)
                split_hi(g0 + next(split_at))
                for e in es:
                    gelu_sigmoid(e)
                if pair == 0:
                    for g in range(4):
                        if g < 3:
                            act.wait_ge(p_done, g + 1)
                        else:
                            act.wait_ge(w_used, g0 + MIX_P + 1)
                        copy(h_hi[:, 4 + g, :], ps[:, g, :],
                             cols[:, POOL_SCALE + g:POOL_SCALE + g + 1]).then_inc(yhi_ready, 1)
                for e in es:
                    act.wait_ge(gelu_ready, e + 1)
                    nc.scalar.activation(body(tile_s, e % 2), body(tile_u, e % 2),
                                         ACT.Square).then_inc(vsquare_ready, 1)
                split_hi(g0 + next(split_at))
                for e in es:
                    act.wait_ge(vnorm_ready, e + 1)
                    act.wait_ge(vzero_set, 2)
                    for half in range(2):
                        source = body(tile_u, e % 2).rearrange("p (q e d) -> p q e d", e=2, d=HEAD_DIM)
                        copy(v_halves(h_hi, e, half), source[:, :, half, :]).then_inc(vhi_ready, 1)
            for pair in range(2):
                es = (2 * pair, 2 * pair + 1)
                for e in es:
                    gelu_square(TT + e)
                for e in es:
                    gelu_sigmoid(TT + e)
                split_hi(g0 + next(split_at))
                for e in es:
                    act.wait_ge(ya_ready, e + 1)
                    copy(h_hi[:, e, :], body(tile_g, e % 2)).then_inc(yhi_ready, 1)
            split_hi(g0 + next(split_at))
            projection(g0 + MIX_OUT, QUAD_M, KD, 2 * KD, GAIN_FFN[1])
            gate_up(1)
            projection(FFN_GRAIN[1] + GATE_UP, QUAD_F, 2 * KD, 3 * KD, 0, has_hi=False)
            copy_r(3)

        @block.vector
        def _(dve):
            def multiply(out, a, b):
                return nc.vector.tensor_tensor(out, a, b, ALU.mult)

            def less(out, a, hi):
                return nc.vector.tensor_tensor(out, a, hi.bitcast(F32), ALU.subtract)

            def split_lo(n):
                dve.wait_ge(whi_ready, n + 1)
                s = SLOT_OF[n]
                cut = TT * P if n == MIX_GRAIN + MIX_P else GRAIN
                less(w_lo[:, s, 0:cut], w_raw[:, s, 0:cut], w_hi[:, s, 0:cut]).then_inc(wlo_ready, 1)

            def gained_lo(c, count, gain):
                dve.wait_ge(xhi_ready, count + c + 1)
                nc.vector.scalar_tensor_tensor(
                    out=x_lo[:, c, :], in0=x_res[:, c, :], scalar=cols[:, gain + c:gain + c + 1],
                    in1=x_hi[:, c, :].bitcast(F32), op0=ALU.mult, op1=ALU.subtract).then_inc(xlo_ready, 1)

            def add_residual(c, before, quad_end, bank, scale):
                if c % HALF < HALF - 1:
                    dve.wait_ge(chunk_done, (HALF - 1) * before + c % HALF + 1)
                else:
                    dve.wait_ge(w_used, quad_end)
                nc.vector.scalar_tensor_tensor(
                    out=x_res[:, c, :], in0=ps[:, bank, :], scalar=scale, in1=x_res[:, c, :],
                    op0=ALU.mult, op1=ALU.add).then_inc(xnew_ready, 1)

            def mean(norm):
                dve.wait_ge(colsum_done, norm + 1)
                nc.vector.tensor_scalar(mean_col[:, :], ps[:, COL_BANK, 0:TT], 1.0 / D_MODEL, EPS,
                                        ALU.mult, ALU.add).then_inc(mean_ready, 1)

            def diagonal(norm):
                dve.wait_ge(rcol_ready, norm + 1)
                for t in range(TT):
                    last = nc.vector.tensor_scalar(tile_u[:, 0, PAD + t * P:PAD + (t + 1) * P],
                                                   ident[:, :], r_col[:, t:t + 1], None, ALU.mult)
                last.then_inc(diag_ready, 1)

            def gate_times_r(b, used):
                dve.wait_ge(w_used, used)
                multiply(body(tile_g, b), ps[:, 2 * b, :], r_row[:, :]).then_inc(gate_ready, 1)
                multiply(body(tile_u, b), ps[:, 2 * b + 1, :], r_row[:, :]).then_inc(up_ready, 1)

            def hidden(j, b):
                dve.wait_ge(silu_ready, j + 1)
                dve.wait_ge(up_ready, j + 1)
                multiply(body(tile_u, b), body(tile_u, b), body(tile_g, b)).then_inc(hid_ready, 1)

            def hidden_lo(j, b, at):
                dve.wait_ge(hhi_ready, j + 1)
                less(h_lo[:, at, :], body(tile_u, b), h_hi[:, at, :]).then_inc(hlo_ready, 1)

            def gate_up(f):
                g0 = FFN_GRAIN[f]
                u0, _, norm = ffn_count(f)
                mean(norm)
                diagonal(norm)
                dve.wait_ge(rrow_ready, norm + 1)

                def straight(j):
                    gate_times_r(j % 2, g0 + 2 * j + 2)
                    split_lo(g0 + 4 + 2 * j)
                    hidden(u0 + j, j % 2)
                    split_lo(g0 + 5 + 2 * j)
                    hidden_lo(u0 + j, j % 2, j)

                def split_ahead(i, c):
                    dve.wait_ge(whi_ready, g0 + c + 5 + SLOTS * i)
                    s = SLOT_OF[g0 + c]
                    less(w_lo[:, s, :], w_raw[:, s, :], w_hi[:, s, :]).then_inc(wlo_ready, 1)

                straight(0)
                straight(1)
                last = KF // 2 - 1
                with dve.Fori(1, last) as i:
                    for j in range(2):
                        gate_times_r(j, g0 + 2 * j + 2 + SLOTS * i)
                        split_ahead(i, 2 * j)
                        hidden(u0 + j + 2 * i, j)
                        split_ahead(i, 2 * j + 1)
                        hidden_lo(u0 + j + 2 * i, j, j + 2 * i)
                straight(KF - 2)
                straight(KF - 1)

            def projection(n0, quad, c0, bank0, scale, gain, has_hi=True):
                def evacuate(c):
                    q = c // HALF
                    add_residual(c, c0 // HALF + q, n0 + (q + 1) * quad, (bank0 if c < HALF else 4 - bank0) + c % HALF, scale)
                    if has_hi:
                        gained_lo(c, c0 + KD, gain)

                for step in range(2 * quad):
                    q, g = divmod(step, quad)
                    if step == 2 * quad - 1:
                        for c in range(HALF, KD):
                            evacuate(c)
                    if q == 1 and g < HALF and step != 2 * quad - 1:
                        evacuate(g)
                    if q == 1 and quad == HALF and step == 2 * quad - 2:
                        evacuate(g + 1)
                    if n0 + step + SLOTS < N_GRAINS:
                        split_lo(n0 + step + SLOTS)

            dve.wait_ge(consts_loaded, 48)
            for c in range(KD):
                gained_lo(c, 0, GAIN_FFN[0])
                if c in (1, 3):
                    split_lo(c - 1)
                    split_lo(c)
            dve.wait_ge(ranks_set, 1)
            nc.vector.reciprocal(inv_count[:, :], inv_count[:, :]).then_inc(inv_set, 1)
            dve.wait_ge(pads_set, 3)
            gate_up(0)
            projection(GATE_UP, QUAD_F, 0, 4, 0.5, GAIN_MIX)

            g0 = MIX_GRAIN
            split_lo(g0 + 4)
            mean(1)
            diagonal(1)
            split_lo(g0 + 5)
            dve.wait_ge(rrow_ready, 2)
            split_lo(g0 + 6)
            split_lo(g0 + 7)
            for g, window in enumerate(POOL_WINDOWS):
                b = g % 2
                dve.wait_ge(w_used, g0 + MIX_Z + g + 1)
                multiply(body(tile_g, b), ps[:, g, :], r_row[:, :]).then_inc(z_ready, 1)
                dve.wait_ge(windows_ready, g + 1)
                head = tile_u[:, b, PAD:PAD + window - 1]
                if g == 0:
                    dve.wait_ge(inv_set, 1)
                nc.vector.scalar_tensor_tensor(out=head, in0=head, scalar=float(window),
                                               in1=inv_count[:, 0:window - 1], op0=ALU.mult,
                                               op1=ALU.mult).then_inc(head_fixed, 1)
                dve.wait_ge(head_fixed, g + 1)
                nc.vector.scalar_tensor_tensor(out=body(tile_s, b), in0=body(tile_u, b), scalar=1.0 / window,
                                               in1=body(tile_g, b), op0=ALU.mult,
                                               op1=ALU.subtract).then_inc(diff_ready, 1)
                dve.wait_ge(dhi_ready, g + 1)
                less(h_lo[:, DIFF + g, :], body(tile_s, b), h_hi[:, DIFF + g, :]).then_inc(dlo_ready, 1)
            for i in range(3):
                split_lo(g0 + 8 + i)

            def cubic(e):
                dve.wait_ge(argsq_ready, e + 1)
                nc.vector.scalar_tensor_tensor(out=body(tile_s, e % 2), in0=body(tile_s, e % 2), scalar=1.0,
                                               in1=body(tile_g, e % 2), op0=ALU.add,
                                               op1=ALU.mult).then_inc(cubic_ready, 1)

            split_at = iter((11, 12, 13, 14, 15, 16, 17))
            dve.wait_ge(w_used, g0 + MIX_V + 4)
            for pair in range(2):
                es = (2 * pair, 2 * pair + 1)
                for e in es:
                    nc.vector.tensor_scalar(body(tile_g, e % 2), ps[:, 4 + e, :], r_col[:, e:e + 1], None,
                                            ALU.mult).then_inc(arg_ready, 1)
                split_lo(g0 + next(split_at))
                for e in es:
                    cubic(e)
                if pair == 0:
                    for g in range(4):
                        dve.wait_ge(yhi_ready, g + 1)
                        nc.vector.scalar_tensor_tensor(
                            out=h_lo[:, 4 + g, :], in0=ps[:, g, :],
                            scalar=cols[:, POOL_SCALE + g:POOL_SCALE + g + 1],
                            in1=h_hi[:, 4 + g, :].bitcast(F32), op0=ALU.mult,
                            op1=ALU.subtract).then_inc(ylo_ready, 1)
                for e in es:
                    dve.wait_ge(vsquare_ready, e + 1)
                    nc.vector.tensor_reduce(v_sums[:, e % 2, :],
                                            body(tile_s, e % 2).rearrange("p (h d) -> p h d", d=HEAD_DIM),
                                            AX_X, ALU.add).then_inc(vsum_ready, 1)
                for e in es:
                    dve.wait_ge(vsum_ready, e + 1)
                    nc.vector.tensor_scalar(v_sums[:, e % 2, :], v_sums[:, e % 2, :], 1.0 / HEAD_DIM, EPS,
                                            ALU.mult, ALU.add).then_inc(vmean_ready, 1)
                split_lo(g0 + next(split_at))
                for e in es:
                    dve.wait_ge(vscale_ready, e + 1)
                    v = body(tile_u, e % 2).rearrange("p (h d) -> p h d", d=HEAD_DIM)
                    scale = v_scale[:, e % 2, :].unsqueeze(2).to_broadcast([P, A_HEADS, HEAD_DIM])
                    multiply(v, v, scale).then_inc(vnorm_ready, 1)
                for e in es:
                    for half in range(2):
                        dve.wait_ge(vhi_ready, 2 * e + half + 1)
                        source = body(tile_u, e % 2).rearrange("p (q e d) -> p q e d", e=2, d=HEAD_DIM)
                        less(v_halves(h_lo, e, half), source[:, :, half, :],
                             v_halves(h_hi, e, half)).then_inc(vlo_ready, 1)
            for pair in range(2):
                es = (2 * pair, 2 * pair + 1)
                for e in es:
                    dve.wait_ge(w_used, g0 + (MIX_U + e if e < 3 else MIX_U3) + 1)
                    if e >= 2:
                        dve.wait_ge(ylo_ready, 4 + e - 1)
                    multiply(body(tile_g, e % 2), ps[:, e, :], r_row[:, :]).then_inc(arg_ready, 1)
                for e in es:
                    cubic(TT + e)
                split_lo(g0 + next(split_at))
                for e in es:
                    if e < 3:
                        dve.wait_ge(s_done, e + 1)
                    else:
                        dve.wait_ge(w_used, g0 + MIX_S + 1)
                    dve.wait_ge(gelu_ready, TT + e + 1)
                    nc.vector.scalar_tensor_tensor(
                        out=body(tile_s, e % 2).rearrange("p (n t) -> p n t", t=P),
                        in0=ps[:, 4 + e, :].rearrange("p (n t) -> p n t", t=P),
                        scalar=cols[:, GAIN_V + e:GAIN_V + e + 1],
                        in1=bias_bc[:, e:e + 1, :].to_broadcast([P, TT, P]), op0=ALU.mult,
                        op1=ALU.add).then_inc(spat_ready, 1)
                for e in es:
                    dve.wait_ge(spat_ready, e + 1)
                    multiply(body(tile_g, e % 2), body(tile_s, e % 2), body(tile_u, e % 2)).then_inc(ya_ready, 1)
                for e in es:
                    dve.wait_ge(yhi_ready, 4 + e + 1)
                    less(h_lo[:, e, :], body(tile_g, e % 2), h_hi[:, e, :]).then_inc(ylo_ready, 1)
            split_lo(g0 + next(split_at))
            projection(g0 + MIX_OUT, QUAD_M, KD, 0, 1.0, GAIN_FFN[1])
            gate_up(1)
            projection(FFN_GRAIN[1] + GATE_UP, QUAD_F, 2 * KD, 4, 0.5, 0, has_hi=False)
            mean(3)
            diagonal(3)
            dve.wait_ge(rrow_ready, 4)
            for c in range(KD):
                nc.vector.scalar_tensor_tensor(
                    out=x_res[:, c, :], in0=x_res[:, c, :], scalar=cols[:, GAIN_FINAL + c:GAIN_FINAL + c + 1],
                    in1=r_row[:, :], op0=ALU.mult, op1=ALU.mult).then_inc(out_ready, 1)

        @block.gpsimd
        def _(pool):
            for n, tile in enumerate((tile_g, tile_s, tile_u)):
                nc.gpsimd.memset(tile[:, :, 0:PAD], 0.0).then_inc(pads_set, 1)
            nc.gpsimd.memset(minus_half[:, :], -0.5).then_inc(pads_set, 1)
            nc.gpsimd.iota(inv_count[:, :], pattern=[[1, PAD]], base=1, channel_multiplier=0,
                           allow_small_or_imprecise_dtypes=True).then_inc(ranks_set, 1)
            nc.gpsimd.memset(ones[:, :], 1.0).then_inc(pads_set, 1)
            pool.wait_ge(pads_set, 5)
            nc.gpsimd.affine_select(out=ident[:, :], in_=ones[:, :], compare_op=ALU.is_equal, fill=0.0,
                                    base=0, pattern=[[1, P]], channel_multiplier=-1).then_inc(consts_set, 1)

            def add_squares(count):
                for c in range(KD):
                    pool.wait_ge(square_ready, count + c + 1)
                    if c == 0:
                        nc.gpsimd.sem_inc(squares_added, 1)
                        continue
                    pool.wait_ge(squares_added, count + c)
                    nc.gpsimd.tensor_tensor(square_sum[:, :], square_sum[:, :], body(tile_s, c % 2),
                                            ALU.add).then_inc(squares_added, 1)

            def root(norm):
                pool.wait_ge(mean_ready, norm + 1)
                nc.gpsimd.tensor_tensor(r_col[:, :], mean_col[:, :], minus_half[:, 0:TT],
                                        ALU.pow).then_inc(rcol_ready, 1)

            def silu(j, b):
                pool.wait_ge(sig_ready, j + 1)
                nc.gpsimd.tensor_tensor(body(tile_g, b), body(tile_g, b), body(tile_s, b),
                                        ALU.mult).then_inc(silu_ready, 1)

            def gate_up(f):
                u0, _, norm = ffn_count(f)
                root(norm)
                with pool.Fori(0, KF // 2) as i:
                    for j in range(2):
                        silu(u0 + j + 2 * i, j)

            def gelu(e):
                pool.wait_ge(gsig_ready, e + 1)
                nc.gpsimd.tensor_tensor(body(tile_u, e % 2), body(tile_g, e % 2), body(tile_s, e % 2),
                                        ALU.mult).then_inc(gelu_ready, 1)

            add_squares(0)
            gate_up(0)
            add_squares(KD)
            pool.wait_ge(w_used, MIX_GRAIN)
            for h in (h_hi, h_lo):
                nc.gpsimd.memset(h[:, VPAD:VPAD + 2 * TT, :].bitcast(F32), 0.0).then_inc(vzero_set, 1)
            root(1)
            steps = 0
            for g, window in enumerate(POOL_WINDOWS):
                b = g % 2
                pool.wait_ge(z_ready, g + 1)
                source, width, turn = tile_g, 1, g % 2
                while width < window:
                    doublings_left = (window // width).bit_length() - 1
                    target = tile_u if doublings_left % 2 else tile_s
                    if width > 1:
                        pool.wait_ge(pool_step, steps)
                    inst = nc.gpsimd.tensor_tensor(target[:, b, PAD:PAD + SEQ], source[:, b, PAD:PAD + SEQ],
                                                   source[:, b, PAD - width:PAD + SEQ - width], ALU.add)
                    width *= 2
                    if width < window:
                        inst.then_inc(pool_step, 1)
                        steps += 1
                    else:
                        inst.then_inc(windows_ready, 1)
                    source = target
            p, j = PAIR_OF[MIX_GRAIN + MIX_S]
            pool.wait_ge(weights_loaded[p % 2], 16 * (p // 2 + 1))
            spatial = w_raw[:, SLOT_OF[MIX_GRAIN + MIX_S], :].rearrange("p (h t) -> p h t", t=P)
            nc.gpsimd.affine_select(out=spatial, in_=spatial, compare_op=ALU.is_ge, fill=0.0, base=0,
                                    pattern=[[0, A_HEADS], [1, P]], channel_multiplier=-1).then_inc(masked, 1)
            for pair in range(2):
                es = (2 * pair, 2 * pair + 1)
                for e in es:
                    gelu(e)
                for e in es:
                    pool.wait_ge(vmean_ready, e + 1)
                    nc.gpsimd.tensor_tensor(v_scale[:, e % 2, :], v_sums[:, e % 2, :], minus_half[:, :],
                                            ALU.pow).then_inc(vscale_ready, 1)
            for e in range(TT):
                gelu(TT + e)
            add_squares(2 * KD)
            gate_up(1)
            add_squares(3 * KD)
            root(3)


def kernel(**inputs):
    import numpy as np
    import concourse.bacc as bacc
    from concourse.bass_utils import run_bass_kernel_spmd

    a = {k: np.asarray(v) for k, v in inputs.items()}

    def by_rows(w, columns, k):
        return w.reshape(k, P, columns).transpose(1, 0, 2).reshape(P, k * columns)

    def ffn(tag):
        gate, up, down = (a[f"{tag}_w_{n}"][0] for n in ("gate", "up", "down"))
        grains = [by_rows(w[:, j * P:(j + 1) * P], P, KD) for j in range(KF) for w in (gate, up)]
        return grains + projection(down, range(QUAD_F))

    def projection(w, order):
        half = HALF * P
        return [by_rows(w[2 * g * P:2 * (g + 1) * P, q * half:(q + 1) * half], half, 2)
                for q in range(2) for g in order]

    w_in = a["w_in"][0]
    u_w, v_w, z_w = (w_in[:, n * A_WIDTH:(n + 1) * A_WIDTH] for n in range(3))
    tile = lambda w, i: by_rows(w[:, i * P:(i + 1) * P], P, KD)
    pool_w = np.zeros((P, GRAIN), np.float32)
    pool_w[:, 0:TT * P] = by_rows(a["pool_w"][0].reshape(4 * P, P), P, 4)
    spatial = a["gmlp_w_s"][0].transpose(2, 0, 1).reshape(P, GRAIN)
    grains = ffn("ffn1")
    grains += [tile(z_w, i) for i in range(4)]
    grains += [by_rows(v_w[2 * g * P:2 * (g + 1) * P], A_WIDTH, 2) for g in range(4)]
    grains += [pool_w] + [tile(u_w, i) for i in range(3)] + [spatial, tile(u_w, 3)]
    grains += projection(a["w_out"][0], (2, 3, 0, 1))
    grains += ffn("ffn2")
    stream = np.zeros((len(PAIRS), P, PAIR * GRAIN), np.float32)
    for n, g in enumerate(grains):
        p, j = PAIR_OF[n]
        stream[p, :, j * GRAIN:(j + 1) * GRAIN] = g
    columns = np.concatenate([a[k].reshape(-1, P) for k in (
        "ffn1_norm", "ffn2_norm", "mix_norm", "final_norm", "gmlp_v_norm", "pool_scale")]).T
    bias = a["gmlp_b_s"][0].reshape(A_HEADS // 2, 2, P).transpose(1, 0, 2)
    arrays = {
        "in_x": np.ascontiguousarray(a["x"][0].T).reshape(KD, P, SEQ),
        "in_stream": stream,
        "in_columns": np.ascontiguousarray(columns),
        "in_bias": np.ascontiguousarray(bias),
    }
    nc = bacc.Bacc("TRN2", target_bir_lowering=False, num_devices=1)
    args = [nc.dram_tensor(name, v.shape, F32, kind="ExternalInput").ap() for name, v in arrays.items()]
    args.append(nc.dram_tensor("out_t", (KD, P, SEQ), F32, kind="ExternalOutput").ap())
    build_block(nc, *args)
    r = run_bass_kernel_spmd(nc, [arrays], core_ids=[0])
    return np.ascontiguousarray(r.results[0]["out_t"].reshape(D_MODEL, SEQ).T)[None]
```

```python
from contextlib import ExitStack

import concourse.bass as bass
from concourse import mybir

F32 = mybir.dt.float32
F32R = mybir.dt.float32r
ALU = mybir.AluOpType
ACT = mybir.ActivationFunctionType
AX_X = mybir.AxisListType.X

P = 128
D_MODEL = 1024
SEQ = 512
D_FF = 2816
A_WIDTH = 512
A_HEADS = 8
HEAD_DIM = A_WIDTH // A_HEADS
POOL_WINDOWS = (2, 4, 8, 16)
EPS = 1e-6
GELU_CUBIC = 0.044715
GELU_SLOPE = 2.0 * (2.0 / 3.141592653589793) ** 0.5

KD = D_MODEL // P
KF = D_FF // P
TT = SEQ // P
HALF = KD // 2
GRAIN = 8 * P
SLOTS = 4
PAIR = 2
PAD = 16

QUAD_F = KF // PAIR
QUAD_M = KD // PAIR
GATE_UP = 2 * KF
FFN_GRAINS = GATE_UP + 2 * QUAD_F
MIX_Z, MIX_V, MIX_P, MIX_U, MIX_S, MIX_OUT = 0, 4, 8, 9, 13, 14
MIX_GRAINS = MIX_OUT + 2 * QUAD_M


def plan_stream():
    slot_of, pair_of, pairs = [], [], []
    slot = 0
    for n, runs in ((0, (GATE_UP, QUAD_F, QUAD_F)), (1, (MIX_GRAINS,)), (2, (GATE_UP, QUAD_F, QUAD_F))):
        for run in runs:
            for g in range(0, run, PAIR):
                k = min(PAIR, run - g)
                pairs.append((len(slot_of), k))
                for j in range(k):
                    slot_of.append((slot + j) % SLOTS)
                    pair_of.append((len(pairs) - 1, j))
                slot = (slot + PAIR) % SLOTS
    return slot_of, pair_of, pairs


SLOT_OF, PAIR_OF, PAIRS = plan_stream()
N_GRAINS = len(SLOT_OF)
FFN_GRAIN = (0, FFN_GRAINS + MIX_GRAINS)
MIX_GRAIN = FFN_GRAINS


def same_slot_before(n):
    return next((m for m in range(n - 1, -1, -1) if SLOT_OF[m] == SLOT_OF[n]), None)


def plan_splits():
    freed, last = [[] for _ in range(N_GRAINS)], 0
    for n in range(SLOTS, N_GRAINS):
        last = max(last, same_slot_before(n))
        freed[last].append(n)
    return freed


FREED = plan_splits()

START = (("x", 0), ("w", 0), ("x", 1), ("x", 2), ("x", 3), ("w", 1), ("square", 0), ("x", 4), ("w", 2),
         ("square", 1), ("x", 5), ("x", 6), ("w", 3), ("square", 2), ("x", 7), ("square", 3))


def build_block(nc: bass.Bass, x_t, stream, columns, spatial_bias, out_t):
    with ExitStack() as ctx:
        def sb(name, shape, dt=F32):
            return ctx.enter_context(nc.sbuf_tensor(name, shape, dt))

        def sem(name):
            return ctx.enter_context(nc.semaphore(name))

        x_res = sb("x_res", [P, KD, SEQ])
        x_hi = sb("x_hi", [P, KD, SEQ], F32R)
        x_lo = sb("x_lo", [P, KD, SEQ], F32R)
        h_hi = sb("h_hi", [P, KF, SEQ], F32R)
        h_lo = sb("h_lo", [P, KF, SEQ], F32R)
        DIFF = KD
        w_raw = sb("w_raw", [P, SLOTS, GRAIN])
        w_hi = sb("w_hi", [P, SLOTS, GRAIN], F32R)
        w_lo = sb("w_lo", [P, SLOTS, GRAIN], F32R)
        tile_g = sb("tile_g", [P, 2, PAD + SEQ])
        tile_s = sb("tile_s", [P, 2, PAD + SEQ])
        tile_u = sb("tile_u", [P, 2, PAD + SEQ])
        square_sum = sb("square_sum", [P, SEQ])
        r_row = sb("r_row", [P, SEQ])
        r_col = sb("r_col", [P, TT])
        mean_col = sb("mean_col", [P, TT])
        v_sums = sb("v_sums", [P, 2, A_HEADS])
        v_scale = sb("v_scale", [P, 2, A_HEADS])
        minus_half = sb("minus_half", [P, A_HEADS])
        ident = sb("ident", [P, P])
        ones = sb("ones", [P, P])
        inv_count = sb("inv_count", [P, PAD])
        bias_bc = sb("bias_bc", [P, A_HEADS // 2, P])
        cols = sb("cols", [P, 4 * KD + 8])
        GAIN_MIX, GAIN_FINAL, GAIN_V, POOL_SCALE = 2 * KD, 3 * KD, 4 * KD, 4 * KD + 4
        GAIN_FFN = (0, KD)

        ps = ctx.enter_context(nc.psum_tensor("ps", [P, 8, SEQ], F32))
        R_BANK, COL_BANK = 4, 5

        x_loaded = [sem(f"x_loaded{c}") for c in range(KD)]
        consts_loaded = sem("consts_loaded")
        pads_set = sem("pads_set")
        consts_set = sem("consts_set")
        bias_loaded = sem("bias_loaded")
        ranks_set = sem("ranks_set")
        inv_set = sem("inv_set")
        weights_loaded = [sem(f"weights_loaded{h}") for h in range(2)]
        masked = sem("masked")
        first_loaded = [sem(f"first_loaded{i}") for i in range(3)]
        first_whi = sem("first_whi")
        first_wlo = sem("first_wlo")
        whi_ready = sem("whi_ready")
        wlo_ready = sem("wlo_ready")
        w_used = sem("w_used")
        gate_ready = sem("gate_ready")
        up_ready = sem("up_ready")
        sig_ready = sem("sig_ready")
        silu_ready = sem("silu_ready")
        hid_ready = sem("hid_ready")
        hhi_ready = sem("hhi_ready")
        hlo_ready = sem("hlo_ready")
        chunk_done = sem("chunk_done")
        xnew_ready = sem("xnew_ready")
        xhi_ready = sem("xhi_ready")
        xlo_ready = sem("xlo_ready")
        square_ready = sem("square_ready")
        squares_added = sem("squares_added")
        colsum_done = sem("colsum_done")
        mean_ready = sem("mean_ready")
        rcol_ready = sem("rcol_ready")
        diag_ready = sem("diag_ready")
        rowsum_done = sem("rowsum_done")
        rrow_ready = sem("rrow_ready")
        p_done = sem("p_done")
        s_done = sem("s_done")
        window_step = sem("window_step")
        diff_ready = sem("diff_ready")
        dhi_ready = sem("dhi_ready")
        dlo_ready = sem("dlo_ready")
        yhi_ready = sem("yhi_ready")
        ylo_ready = sem("ylo_ready")
        arg_ready = sem("arg_ready")
        argsq_ready = sem("argsq_ready")
        cubic_ready = sem("cubic_ready")
        gsig_ready = sem("gsig_ready")
        gelu_ready = sem("gelu_ready")
        vsquare_ready = sem("vsquare_ready")
        vsum_ready = sem("vsum_ready")
        vmean_ready = sem("vmean_ready")
        vscale_ready = sem("vscale_ready")
        vnorm_ready = sem("vnorm_ready")
        spat_ready = sem("spat_ready")
        ya_ready = sem("ya_ready")
        out_ready = sem("out_ready")
        out_stored = sem("out_stored")

        def body(tile, b):
            return tile[:, b, PAD:PAD + SEQ]

        def gelu_u(q):
            return body((tile_g, tile_u)[q // 2], q % 2)

        def ffn_count(f):
            return KF * f, 2 * KD * f, 2 * f

        block = ctx.enter_context(nc.Block())

        @block.sync
        def _(sp):
            def load_pair(p):
                first, k = PAIRS[p]
                before = [same_slot_before(first + j) for j in range(k)]
                if before[0] is not None:
                    sp.wait_ge(wlo_ready, max(before) + 1)
                if MIX_GRAIN + MIX_S in before:
                    sp.wait_ge(w_used, MIX_GRAIN + MIX_S + 1)
                s = SLOT_OF[first]
                sp.dma_start(w_raw[:, s:s + k, :], stream[p, :, 0:k * GRAIN]).then_inc(
                    weights_loaded[p % 2], 16)

            sp.dma_start(cols[:, :], columns).then_inc(consts_loaded, 16)
            for what, n in START:
                if what == "x":
                    sp.dma_start(x_res[:, n, :], x_t[n]).then_inc(x_loaded[n], 16)
                if what == "w":
                    at, a = n % 2, n // 2 * (GRAIN // 2)
                    sp.dma_start(w_raw[:, at, a:a + GRAIN // 2],
                                 stream[0, :, at * GRAIN + a:at * GRAIN + a + GRAIN // 2]).then_inc(
                        first_loaded[n] if n < 3 else weights_loaded[0], 16)
            for f in range(2):
                g0 = FFN_GRAIN[f]
                p0 = PAIR_OF[g0][0]
                if f == 1:
                    load_pair(p0)
                load_pair(p0 + 1)
                if f == 0:
                    for e in range(2):
                        sp.dma_start(bias_bc[e * HEAD_DIM:(e + 1) * HEAD_DIM, :, :],
                                     spatial_bias[e:e + 1, :, :].to_broadcast(
                                         [HEAD_DIM, A_HEADS // 2, P])).then_inc(bias_loaded, 16)
                with sp.Fori(1, KF // 2) as i:
                    for u in range(2):
                        s = SLOT_OF[g0 + PAIR * u]
                        sp.wait_ge(wlo_ready, g0 + PAIR * u - 2 + SLOTS * i)
                        sp.dma_start(w_raw[:, s:s + PAIR, :], stream[p0 + u + 2 * i, :, :]).then_inc(
                            weights_loaded[(p0 + u) % 2], 16)
                end = PAIR_OF[FFN_GRAIN[1]][0] if f == 0 else len(PAIRS)
                for p in range(p0 + KF, end):
                    load_pair(p)
            for c in range(KD):
                sp.wait_ge(out_ready, c + 1)
                sp.dma_start(out_t[c], x_res[:, c, :]).then_inc(out_stored, 16)
            sp.wait_ge(out_stored, 16 * KD)

        @block.tensor
        def _(pe):
            def product(out, stat, mov, start, stop):
                (s_hi, s_lo), (m_hi, m_lo) = stat, mov
                nc.tensor.matmul(out, s_hi, m_hi, start=start, stop=False)
                nc.tensor.matmul(out, s_hi, m_lo, start=False, stop=False)
                return nc.tensor.matmul(out, s_lo, m_hi, start=False, stop=stop)

            def weights(slot, a, n=P):
                return w_hi[:, slot, a:a + n], w_lo[:, slot, a:a + n]

            def chunk(pair, k, a=0, n=SEQ):
                return pair[0][:, k, a:a + n], pair[1][:, k, a:a + n]

            XS, HS = (x_hi, x_lo), (h_hi, h_lo)

            def unit(slot, bank, fresh=None, between=None):
                for quarter in range(4):
                    half, w = divmod(quarter, 2)
                    if between and quarter in between:
                        between[quarter](quarter)
                    for k in range(half * HALF, (half + 1) * HALF):
                        if fresh is not None and w == 0:
                            pe.wait_ge(xlo_ready, fresh + k + 1)
                        last = product(ps[:, bank + w, :], weights(slot[w], k * P), chunk(XS, k),
                                       k == 0, k == KD - 1)
                    if half:
                        last.then_inc(w_used, 1)

            def column_sums(norm):
                apart = 2 if norm == 3 else 0
                for n in range(1 + apart):
                    source = square_sum[:, :] if n == 0 else body(tile_s, (KD - apart + n - 1) % 2)
                    if n == 0:
                        pe.wait_ge(squares_added, KD * (norm + 1) - apart)
                    else:
                        pe.wait_ge(square_ready, KD * (norm + 1) - apart + n)
                    for t in range(TT):
                        last = nc.tensor.matmul(ps[:, COL_BANK, t:t + 1], source[:, t * P:(t + 1) * P],
                                                ones[:, 0:1], start=n == 0 and t == 0, stop=n == apart,
                                                skip_group_check=True)
                last.then_inc(colsum_done, 1)

            def row_scale(norm):
                for t in range(TT):
                    cut = slice(t * P, (t + 1) * P)
                    pe.wait_ge(diag_ready, TT * norm + t + 1)
                    last = nc.tensor.matmul(ps[:, R_BANK, cut], ones[:, :], body(tile_u, 0)[:, cut],
                                            start=True, stop=True)
                last.then_inc(rowsum_done, 1)

            def gate_up(f):
                g0 = FFN_GRAIN[f]
                u0, c0, norm = ffn_count(f)
                slots = [(SLOT_OF[g0 + 2 * u], SLOT_OF[g0 + 2 * u + 1]) for u in range(2)]

                def first_weights(quarter):
                    pe.wait_ge(*((first_wlo, quarter + 1) if quarter < 2 else (wlo_ready, quarter - 1)))

                if f == 0:
                    unit(slots[0], 0, fresh=c0, between={q: first_weights for q in range(4)})
                else:
                    pe.wait_ge(wlo_ready, g0 + 2)
                    unit(slots[0], 0, fresh=c0)
                pe.wait_ge(wlo_ready, g0 + 4)
                unit(slots[1], 2, between={2: lambda _: column_sums(norm), 3: lambda _: row_scale(norm)})
                with pe.Fori(1, KF // 2) as i:
                    for u in range(2):
                        pe.wait_ge(wlo_ready, g0 + 2 * u + 2 + SLOTS * i)
                        pe.wait_ge(up_ready, u0 + u - 1 + 2 * i)
                        unit(slots[u], 2 * u)

            def quad_granule(slot, bank, ks, first, last_one):
                for m in range(HALF):
                    for j, k in enumerate(ks):
                        last = product(ps[:, bank(m), :], weights(slot, j * HALF * P + m * P), chunk(HS, k),
                                       first and j == 0, last_one and j == 1)
                    if last_one and m < HALF - 1:
                        last.then_inc(chunk_done, 1)
                return last

            def down(f):
                g0 = FFN_GRAIN[f] + GATE_UP
                u0, _, _ = ffn_count(f)
                with nc.Fori(0, 2, engines=[pe.engine], hint_back_edge=True) as q:
                    for g in range(QUAD_F):
                        pe.wait_ge(wlo_ready, g0 + g + 1 + QUAD_F * q)
                        if g == 0:
                            pe.wait_ge(up_ready, u0 + KF)
                        pe.wait_ge(hlo_ready, u0 + 2 * g + 2)
                        quad_granule(SLOT_OF[g0 + g], lambda m: 4 + m - 4 * q, (2 * g, 2 * g + 1),
                                     g == 0, g == QUAD_F - 1).then_inc(w_used, 1)

            def mixer():
                g0 = MIX_GRAIN

                def tile_of(n, bank, fresh):
                    pe.wait_ge(wlo_ready, g0 + n + 1)
                    for k in range(KD):
                        if fresh:
                            pe.wait_ge(xlo_ready, KD + k + 1)
                        last = product(ps[:, bank, :], weights(SLOT_OF[g0 + n], k * P), chunk(XS, k),
                                       k == 0, k == KD - 1)
                    last.then_inc(w_used, 1)

                for i in range(4):
                    pe.wait_ge(xnew_ready, HALF + i + 1)
                    tile_of(MIX_Z + i, i, i == 0)
                    if i == 0:
                        column_sums(1)
                    if i == 1:
                        row_scale(1)
                pe.wait_ge(rrow_ready, 2)
                for g in range(4):
                    pe.wait_ge(wlo_ready, g0 + MIX_V + g + 1)
                    for t in range(TT):
                        for j in range(2):
                            k = 2 * g + j
                            last = product(ps[:, 4 + t, :], chunk(XS, k, t * P, P),
                                           weights(SLOT_OF[g0 + MIX_V + g], j * SEQ, SEQ),
                                           k == 0, k == KD - 1)
                    last.then_inc(w_used, 1)
                pe.wait_ge(wlo_ready, g0 + MIX_P + 1)
                for g in range(4):
                    pe.wait_ge(dlo_ready, g + 1)
                    last = product(ps[:, g, :], weights(SLOT_OF[g0 + MIX_P], g * P), chunk(HS, DIFF + g),
                                   True, True)
                    last.then_inc(p_done if g < 3 else w_used, 1)
                def spatial(n):
                    pe.wait_ge(vnorm_ready, n + 1)
                    for q in range(A_HEADS // 2):
                        for e in range(2):
                            head = 2 * q + e
                            last = nc.tensor.matmul(
                                ps[e * HEAD_DIM:(e + 1) * HEAD_DIM, 4 + n, q * P:(q + 1) * P],
                                body(tile_u, n % 2)[:, head * HEAD_DIM:(head + 1) * HEAD_DIM],
                                w_raw[:, SLOT_OF[g0 + MIX_S], head * P:(head + 1) * P],
                                start=True, stop=True)
                    last.then_inc(s_done if n < 3 else w_used, 1)

                for i in range(4):
                    pe.wait_ge(ylo_ready, i + 1)
                    tile_of(MIX_U + i, i, False)
                    if i == 1:
                        pe.wait_ge(masked, 1)
                        spatial(0)
                        spatial(1)
                spatial(2)
                spatial(3)
                for q in range(2):
                    for g, (ks, need) in enumerate((((4, 5), 4), ((6, 7), 4), ((0, 1), 6), ((2, 3), 8))):
                        n = g0 + MIX_OUT + QUAD_M * q + g
                        pe.wait_ge(wlo_ready, n + 1)
                        if q == 0:
                            pe.wait_ge(ylo_ready, need)
                        for m in range(HALF):
                            if g == 0 and q == 0:
                                pe.wait_ge(arg_ready, TT + m + 1)
                            if g == 0 and m == 0 and q == 1:
                                pe.wait_ge(spat_ready, TT)
                            for j, k in enumerate(ks):
                                last = product(ps[:, 4 * q + m, :],
                                               weights(SLOT_OF[n], j * HALF * P + m * P), chunk(HS, k),
                                               g == 0 and j == 0, g == QUAD_M - 1 and j == 1)
                            if g == QUAD_M - 1 and m < HALF - 1:
                                last.then_inc(chunk_done, 1)
                        last.then_inc(w_used, 1)

            gate_up(0)
            down(0)
            mixer()
            gate_up(1)
            down(1)
            column_sums(3)
            row_scale(3)

        @block.scalar
        def _(act):
            def copy(out, in_, scale=1.0):
                return nc.scalar.activation(out, in_, ACT.Copy, scale=scale)

            def split_hi(n):
                p, j = PAIR_OF[n]
                act.wait_ge(weights_loaded[p % 2], 16 * (p // 2 + 1))
                if (m := same_slot_before(n)) is not None:
                    act.wait_ge(w_used, m + 1)
                cut = TT * P if n == MIX_GRAIN + MIX_P else GRAIN
                copy(w_hi[:, SLOT_OF[n], 0:cut], w_raw[:, SLOT_OF[n], 0:cut]).then_inc(whi_ready, 1)

            def chunk_hi(c, gain):
                nc.scalar.activation(x_hi[:, c, :], x_res[:, c, :], ACT.Copy,
                                     scale=cols[:, gain + c:gain + c + 1]).then_inc(xhi_ready, 1)

            def chunk_square(c, count):
                if c == 0:
                    nc.scalar.activation(square_sum[:, :], x_res[:, c, :], ACT.Square).then_inc(square_ready, 1)
                else:
                    act.wait_ge(squares_added, count + c - 1)
                    nc.scalar.activation(body(tile_s, c % 2), x_res[:, c, :],
                                         ACT.Square).then_inc(square_ready, 1)

            def copy_r(norm):
                act.wait_ge(rowsum_done, norm + 1)
                copy(r_row[:, :], ps[:, R_BANK, :]).then_inc(rrow_ready, 1)

            def sigmoid_gate(j, b):
                act.wait_ge(gate_ready, j + 1)
                nc.scalar.activation(body(tile_s, b), body(tile_g, b), ACT.Sigmoid).then_inc(sig_ready, 1)

            def hidden_hi(j, b, at):
                act.wait_ge(hid_ready, j + 1)
                copy(h_hi[:, at, :], body(tile_u, b)).then_inc(hhi_ready, 1)

            def gate_up(f):
                g0 = FFN_GRAIN[f]
                u0, _, norm = ffn_count(f)
                for n in range(4, 7):
                    split_hi(g0 + n)
                copy_r(norm)
                sigmoid_gate(u0, 0)
                sigmoid_gate(u0 + 1, 1)
                hidden_hi(u0, 0, 0)
                split_hi(g0 + 7)
                hidden_hi(u0 + 1, 1, 1)
                last = KF // 2 - 1
                p0 = PAIR_OF[g0][0]

                def split_ahead(i, c):
                    p = p0 + c // 2
                    act.wait_ge(weights_loaded[p % 2], 16 * (p // 2 + 2) + 16 * i)
                    act.wait_ge(w_used, g0 + c + 1 + SLOTS * i)
                    s = SLOT_OF[g0 + c]
                    copy(w_hi[:, s, :], w_raw[:, s, :]).then_inc(whi_ready, 1)

                with act.Fori(1, last) as i:
                    for j in range(2):
                        sigmoid_gate(u0 + j + 2 * i, j)
                        split_ahead(i, 2 * j)
                        hidden_hi(u0 + j + 2 * i, j, j + 2 * i)
                        split_ahead(i, 2 * j + 1)
                for j in range(2 * last, KF):
                    sigmoid_gate(u0 + j, j % 2)
                    split_hi(g0 + 4 + 2 * j)
                    hidden_hi(u0 + j, j % 2, j)
                    split_hi(g0 + 5 + 2 * j)

            def chunk_parts(c, count, gain, has_hi):
                if has_hi:
                    chunk_hi(c, gain)
                chunk_square(c, count)

            def projection(n0, quad, c0, count, gain, has_hi=True):
                for step in range(2 * quad):
                    q, g = divmod(step, quad)
                    if step == 2 * quad - 1:
                        for c in range(HALF, KD):
                            act.wait_ge(xnew_ready, c0 + c + 1)
                            chunk_parts(c, count, gain, has_hi)
                    if q == 1 and g < HALF and step != 2 * quad - 1:
                        act.wait_ge(xnew_ready, c0 + g + 1)
                        chunk_parts(g, count, gain, has_hi)
                    if q == 1 and quad == HALF and step == 2 * quad - 2:
                        act.wait_ge(xnew_ready, c0 + g + 2)
                        chunk_parts(g + 1, count, gain, has_hi)
                    for n in FREED[n0 + step]:
                        split_hi(n)

            act.wait_ge(pads_set, 1)
            nc.scalar.activation(v_scale[:, 0, 0:1], tile_g[:, 0, 0:1], ACT.Sigmoid)
            act.wait_ge(consts_loaded, 16)
            for what, n in START:
                if what == "x":
                    act.wait_ge(x_loaded[n], 16)
                    chunk_hi(n, GAIN_FFN[0])
                elif what == "square":
                    chunk_square(n, 0)
                else:
                    act.wait_ge(first_loaded[n] if n < 3 else weights_loaded[0], 16)
                    a = n // 2 * (GRAIN // 2)
                    copy(w_hi[:, n % 2, a:a + GRAIN // 2], w_raw[:, n % 2, a:a + GRAIN // 2]).then_inc(
                        first_whi if n < 2 else whi_ready, 1)
            for n in (2, 3):
                split_hi(n)
            for c in range(4, KD):
                chunk_square(c, 0)
            gate_up(0)
            projection(GATE_UP, QUAD_F, 0, KD, GAIN_MIX)

            g0 = MIX_GRAIN

            def diff_hi(g):
                act.wait_ge(diff_ready, g + 1)
                copy(h_hi[:, DIFF + g, :], body(tile_s, g % 2)).then_inc(dhi_ready, 1)

            split_hi(g0 + 4)
            split_hi(g0 + 5)
            copy_r(1)
            diff_hi(0)
            split_hi(g0 + 6)
            diff_hi(1)
            split_hi(g0 + 7)
            diff_hi(2)
            diff_hi(3)
            for i in range(8, 11):
                split_hi(g0 + i)

            def gelu_square(e):
                act.wait_ge(arg_ready, e + 1)
                if 2 <= e < 6:
                    act.wait_ge(vsum_ready, e - 1)
                if e >= 6:
                    act.wait_ge(ya_ready, e - 5)
                arg = body(tile_g, e % 2) if e < TT else gelu_u(e - TT)
                nc.scalar.activation(body(tile_s, e % 2), arg, ACT.Square,
                                     scale=GELU_CUBIC ** 0.5).then_inc(argsq_ready, 1)

            def gelu_sigmoid(e):
                act.wait_ge(cubic_ready, e + 1)
                nc.scalar.activation(body(tile_s, e % 2), body(tile_s, e % 2), ACT.Sigmoid,
                                     scale=GELU_SLOPE).then_inc(gsig_ready, 1)

            def v_square(e):
                act.wait_ge(gelu_ready, e + 1)
                nc.scalar.activation(body(tile_s, e % 2), body(tile_u, e % 2),
                                     ACT.Square).then_inc(vsquare_ready, 1)

            def ya_hi(q):
                act.wait_ge(ya_ready, q + 1)
                copy(h_hi[:, q, :], gelu_u(q)).then_inc(yhi_ready, 1)

            def pooled_hi(g):
                if g < 3:
                    act.wait_ge(p_done, g + 1)
                else:
                    act.wait_ge(w_used, g0 + MIX_P + 1)
                copy(h_hi[:, 4 + g, :], ps[:, g, :],
                     cols[:, POOL_SCALE + g:POOL_SCALE + g + 1]).then_inc(yhi_ready, 1)

            pooled_hi(0)
            gelu_square(0)
            pooled_hi(1)
            gelu_square(1)
            pooled_hi(2)
            pooled_hi(3)
            gelu_sigmoid(0)
            gelu_sigmoid(1)
            split_hi(g0 + 11)
            split_hi(g0 + 12)
            v_square(0)
            v_square(1)
            gelu_square(2)
            gelu_square(3)
            gelu_sigmoid(2)
            gelu_sigmoid(3)
            act.sem_inc(whi_ready, 1)
            split_hi(g0 + 14)
            v_square(2)
            v_square(3)
            gelu_square(4)
            gelu_square(5)
            gelu_sigmoid(4)
            gelu_sigmoid(5)
            split_hi(g0 + 15)
            ya_hi(0)
            gelu_square(6)
            ya_hi(1)
            gelu_square(7)
            split_hi(g0 + 16)
            gelu_sigmoid(6)
            gelu_sigmoid(7)
            split_hi(g0 + 17)
            ya_hi(2)
            ya_hi(3)
            projection(g0 + MIX_OUT, QUAD_M, KD, 2 * KD, GAIN_FFN[1])
            gate_up(1)
            projection(FFN_GRAIN[1] + GATE_UP, QUAD_F, 2 * KD, 3 * KD, 0, has_hi=False)

        @block.vector
        def _(dve):
            def multiply(out, a, b):
                return nc.vector.tensor_tensor(out, a, b, ALU.mult)

            def less(out, a, hi):
                return nc.vector.tensor_tensor(out, a, hi.bitcast(F32), ALU.subtract)

            def split_lo(n):
                dve.wait_ge(whi_ready, n + 1)
                s = SLOT_OF[n]
                cut = TT * P if n == MIX_GRAIN + MIX_P else GRAIN
                less(w_lo[:, s, 0:cut], w_raw[:, s, 0:cut], w_hi[:, s, 0:cut]).then_inc(wlo_ready, 1)

            def gained_lo(c, count, gain):
                dve.wait_ge(xhi_ready, count + c + 1)
                nc.vector.scalar_tensor_tensor(
                    out=x_lo[:, c, :], in0=x_res[:, c, :], scalar=cols[:, gain + c:gain + c + 1],
                    in1=x_hi[:, c, :].bitcast(F32), op0=ALU.mult, op1=ALU.subtract).then_inc(xlo_ready, 1)

            def add_residual(c, before, quad_end, bank, scale):
                if c % HALF < HALF - 1:
                    dve.wait_ge(chunk_done, (HALF - 1) * before + c % HALF + 1)
                else:
                    dve.wait_ge(w_used, quad_end)
                nc.vector.scalar_tensor_tensor(
                    out=x_res[:, c, :], in0=ps[:, bank, :], scalar=scale, in1=x_res[:, c, :],
                    op0=ALU.mult, op1=ALU.add).then_inc(xnew_ready, 1)

            def mean(norm):
                dve.wait_ge(colsum_done, norm + 1)
                nc.vector.tensor_scalar(mean_col[:, :], ps[:, COL_BANK, 0:TT], 1.0 / D_MODEL, EPS,
                                        ALU.mult, ALU.add).then_inc(mean_ready, 1)

            def diagonal(norm):
                dve.wait_ge(rcol_ready, norm + 1)
                for t in range(TT):
                    nc.vector.tensor_scalar(body(tile_u, 0)[:, t * P:(t + 1) * P], ident[:, :],
                                            r_col[:, t:t + 1], None, ALU.mult).then_inc(diag_ready, 1)

            def gate_times_r(b, used):
                dve.wait_ge(w_used, used)
                multiply(body(tile_g, b), ps[:, 2 * b, :], r_row[:, :]).then_inc(gate_ready, 1)
                multiply(body(tile_u, b), ps[:, 2 * b + 1, :], r_row[:, :]).then_inc(up_ready, 1)

            def hidden(j, b):
                dve.wait_ge(silu_ready, j + 1)
                dve.wait_ge(up_ready, j + 1)
                multiply(body(tile_u, b), body(tile_u, b), body(tile_g, b)).then_inc(hid_ready, 1)

            def hidden_lo(j, b, at):
                dve.wait_ge(hhi_ready, j + 1)
                less(h_lo[:, at, :], body(tile_u, b), h_hi[:, at, :]).then_inc(hlo_ready, 1)

            def gate_up(f):
                g0 = FFN_GRAIN[f]
                u0, _, norm = ffn_count(f)

                def straight(j):
                    gate_times_r(j % 2, g0 + 2 * j + 2)
                    split_lo(g0 + 4 + 2 * j)
                    hidden(u0 + j, j % 2)
                    split_lo(g0 + 5 + 2 * j)
                    hidden_lo(u0 + j, j % 2, j)

                def split_ahead(i, c):
                    dve.wait_ge(whi_ready, g0 + c + 5 + SLOTS * i)
                    s = SLOT_OF[g0 + c]
                    less(w_lo[:, s, :], w_raw[:, s, :], w_hi[:, s, :]).then_inc(wlo_ready, 1)

                split_lo(g0 + 4)
                split_lo(g0 + 5)
                mean(norm)
                diagonal(norm)
                split_lo(g0 + 6)
                dve.wait_ge(rrow_ready, norm + 1)
                for j in range(2):
                    gate_times_r(j, g0 + 2 * j + 2)
                hidden(u0, 0)
                split_lo(g0 + 7)
                hidden_lo(u0, 0, 0)
                hidden(u0 + 1, 1)
                hidden_lo(u0 + 1, 1, 1)
                last = KF // 2 - 1
                with dve.Fori(1, last) as i:
                    for j in range(2):
                        gate_times_r(j, g0 + 2 * j + 2 + SLOTS * i)
                        split_ahead(i, 2 * j)
                        hidden(u0 + j + 2 * i, j)
                        split_ahead(i, 2 * j + 1)
                        hidden_lo(u0 + j + 2 * i, j, j + 2 * i)
                straight(KF - 2)
                straight(KF - 1)

            def projection(n0, quad, c0, bank0, scale, gain, has_hi=True):
                def new(c):
                    q = c // HALF
                    bank = (bank0 if q == 0 else 4 - bank0) + c % HALF
                    add_residual(c, c0 // HALF + q, n0 + (q + 1) * quad, bank, scale)

                def low(c):
                    if has_hi:
                        gained_lo(c, c0 + KD, gain)

                for step in range(2 * quad):
                    q, g = divmod(step, quad)
                    if step == 2 * quad - 1:
                        new(HALF)
                        for c in range(HALF + 1, KD):
                            new(c)
                            low(c - 1)
                        low(KD - 1)
                    if q == 1 and g < HALF and step != 2 * quad - 1:
                        new(g)
                        low(g)
                    if q == 1 and quad == HALF and step == 2 * quad - 2:
                        new(g + 1)
                        low(g + 1)
                    for n in FREED[n0 + step]:
                        split_lo(n)

            for what, n in START:
                if what == "x":
                    gained_lo(n, 0, GAIN_FFN[0])
                elif what == "w":
                    a = n // 2 * (GRAIN // 2)
                    dve.wait_ge(*((first_whi, n + 1) if n < 2 else (whi_ready, n - 1)))
                    cut = slice(a, a + GRAIN // 2)
                    less(w_lo[:, n % 2, cut], w_raw[:, n % 2, cut], w_hi[:, n % 2, cut]).then_inc(
                        first_wlo if n < 2 else wlo_ready, 1)
            split_lo(2)
            split_lo(3)
            dve.wait_ge(ranks_set, 1)
            nc.vector.reciprocal(inv_count[:, :], inv_count[:, :]).then_inc(inv_set, 1)
            dve.wait_ge(consts_set, 1)
            gate_up(0)
            projection(GATE_UP, QUAD_F, 0, 4, 0.5, GAIN_MIX)

            g0 = MIX_GRAIN
            steps = [0]

            def z_scaled(g):
                dve.wait_ge(w_used, g0 + MIX_Z + g + 1)
                if g >= 2:
                    dve.wait_ge(diff_ready, g - 1)
                multiply(body(tile_g, g % 2), ps[:, g, :], r_row[:, :]).then_inc(window_step, 1)
                steps[0] += 1
                z_at[g] = steps[0]

            def z_difference(g):
                b, window = g % 2, POOL_WINDOWS[g]
                if g >= 2:
                    dve.wait_ge(dlo_ready, g - 1)
                dve.wait_ge(window_step, z_at[g])
                source, width = tile_g, 1
                while width < window:
                    left = (window // width).bit_length() - 1
                    target = tile_u if left % 2 else tile_s
                    if width > 1:
                        dve.wait_ge(window_step, steps[0])
                    nc.vector.tensor_tensor(body(target, b), body(source, b),
                                            source[:, b, PAD - width:PAD + SEQ - width],
                                            ALU.add).then_inc(window_step, 1)
                    steps[0] += 1
                    source, width = target, 2 * width
                head = tile_u[:, b, PAD:PAD + window - 1]
                dve.wait_ge(window_step, steps[0])
                nc.vector.scalar_tensor_tensor(out=head, in0=head, scalar=float(window),
                                               in1=inv_count[:, 0:window - 1], op0=ALU.mult,
                                               op1=ALU.mult).then_inc(window_step, 1)
                steps[0] += 1
                dve.wait_ge(window_step, steps[0])
                nc.vector.scalar_tensor_tensor(out=body(tile_s, b), in0=body(tile_u, b), scalar=1.0 / window,
                                               in1=body(tile_g, b), op0=ALU.mult,
                                               op1=ALU.subtract).then_inc(diff_ready, 1)

            def difference_lo(g):
                dve.wait_ge(dhi_ready, g + 1)
                less(h_lo[:, DIFF + g, :], body(tile_s, g % 2), h_hi[:, DIFF + g, :]).then_inc(dlo_ready, 1)

            z_at = {}
            split_lo(g0 + 4)
            mean(1)
            diagonal(1)
            split_lo(g0 + 5)
            dve.wait_ge(rrow_ready, 2)
            dve.wait_ge(inv_set, 1)
            z_scaled(0)
            z_scaled(1)
            z_difference(0)
            split_lo(g0 + 6)
            z_scaled(2)
            z_difference(1)
            difference_lo(0)
            split_lo(g0 + 7)
            difference_lo(1)
            z_difference(2)
            z_scaled(3)
            z_difference(3)
            difference_lo(2)
            difference_lo(3)
            for i in range(8, 11):
                split_lo(g0 + i)

            def cubic(e):
                dve.wait_ge(argsq_ready, e + 1)
                arg = body(tile_g, e % 2) if e < TT else gelu_u(e - TT)
                nc.vector.scalar_tensor_tensor(out=body(tile_s, e % 2), in0=body(tile_s, e % 2), scalar=1.0,
                                               in1=arg, op0=ALU.add,
                                               op1=ALU.mult).then_inc(cubic_ready, 1)

            def v_arg(e):
                if e >= 2:
                    dve.wait_ge(gelu_ready, e - 1)
                nc.vector.tensor_scalar(body(tile_g, e % 2), ps[:, 4 + e, :], r_col[:, e:e + 1], None,
                                        ALU.mult).then_inc(arg_ready, 1)

            def u_arg(q):
                dve.wait_ge(w_used, g0 + (MIX_U + q if q < 2 else MIX_S) + 1)
                if q < 2:
                    dve.wait_ge(gelu_ready, q + 3)
                multiply(gelu_u(q), ps[:, q, :], r_row[:, :]).then_inc(arg_ready, 1)

            def pooled_lo(g):
                dve.wait_ge(yhi_ready, g + 1)
                nc.vector.scalar_tensor_tensor(
                    out=h_lo[:, 4 + g, :], in0=ps[:, g, :], scalar=cols[:, POOL_SCALE + g:POOL_SCALE + g + 1],
                    in1=h_hi[:, 4 + g, :].bitcast(F32), op0=ALU.mult, op1=ALU.subtract).then_inc(ylo_ready, 1)

            def v_mean(e):
                dve.wait_ge(vsquare_ready, e + 1)
                if e >= 2:
                    dve.wait_ge(vscale_ready, e - 1)
                nc.vector.tensor_reduce(v_sums[:, e % 2, :],
                                        body(tile_s, e % 2).rearrange("p (h d) -> p h d", d=HEAD_DIM),
                                        AX_X, ALU.add).then_inc(vsum_ready, 1)
                dve.wait_ge(vsum_ready, e + 1)
                nc.vector.tensor_scalar(v_sums[:, e % 2, :], v_sums[:, e % 2, :], 1.0 / HEAD_DIM, EPS,
                                        ALU.mult, ALU.add).then_inc(vmean_ready, 1)

            def v_normed(e):
                dve.wait_ge(vscale_ready, e + 1)
                v = body(tile_u, e % 2).rearrange("p (h d) -> p h d", d=HEAD_DIM)
                scale = v_scale[:, e % 2, :].unsqueeze(2).to_broadcast([P, A_HEADS, HEAD_DIM])
                multiply(v, v, scale).then_inc(vnorm_ready, 1)

            def spatial_out(q):
                dve.wait_ge(w_used, g0 + MIX_S + 1)
                dve.wait_ge(gelu_ready, TT + q + 1)
                nc.vector.scalar_tensor_tensor(
                    out=body(tile_s, q % 2).rearrange("p (n t) -> p n t", t=P),
                    in0=ps[:, 4:8, q * P:(q + 1) * P],
                    scalar=cols[:, GAIN_V + q:GAIN_V + q + 1],
                    in1=bias_bc[:, q:q + 1, :].to_broadcast([P, TT, P]), op0=ALU.mult,
                    op1=ALU.add).then_inc(spat_ready, 1)

            def gated(q):
                dve.wait_ge(spat_ready, q + 1)
                multiply(gelu_u(q), body(tile_s, q % 2), gelu_u(q)).then_inc(ya_ready, 1)

            def gated_lo(q):
                dve.wait_ge(yhi_ready, 4 + q + 1)
                less(h_lo[:, q, :], gelu_u(q), h_hi[:, q, :]).then_inc(ylo_ready, 1)

            dve.wait_ge(w_used, g0 + MIX_V + 4)
            dve.wait_ge(diff_ready, 4)
            v_arg(0)
            v_arg(1)
            pooled_lo(0)
            pooled_lo(1)
            cubic(0)
            cubic(1)
            pooled_lo(2)
            pooled_lo(3)
            split_lo(g0 + 11)
            split_lo(g0 + 12)
            v_mean(0)
            v_mean(1)
            v_arg(2)
            v_arg(3)
            v_normed(0)
            v_normed(1)
            cubic(2)
            cubic(3)
            dve.sem_inc(wlo_ready, 1)
            split_lo(g0 + 14)
            v_mean(2)
            v_mean(3)
            v_normed(2)
            v_normed(3)
            u_arg(0)
            u_arg(1)
            cubic(4)
            cubic(5)
            split_lo(g0 + 15)
            dve.wait_ge(bias_loaded, 32)
            u_arg(2)
            u_arg(3)
            spatial_out(0)
            spatial_out(1)
            gated(0)
            gated(1)
            gated_lo(0)
            gated_lo(1)
            cubic(6)
            split_lo(g0 + 16)
            cubic(7)
            split_lo(g0 + 17)
            spatial_out(2)
            spatial_out(3)
            gated(2)
            gated(3)
            gated_lo(2)
            gated_lo(3)
            projection(g0 + MIX_OUT, QUAD_M, KD, 0, 1.0, GAIN_FFN[1])
            gate_up(1)
            projection(FFN_GRAIN[1] + GATE_UP, QUAD_F, 2 * KD, 4, 0.5, 0, has_hi=False)
            mean(3)
            diagonal(3)
            dve.wait_ge(rowsum_done, 4)
            for c in range(KD):
                nc.vector.scalar_tensor_tensor(
                    out=x_res[:, c, :], in0=x_res[:, c, :], scalar=cols[:, GAIN_FINAL + c:GAIN_FINAL + c + 1],
                    in1=ps[:, R_BANK, :], op0=ALU.mult, op1=ALU.mult).then_inc(out_ready, 1)

        @block.gpsimd
        def _(pool):
            for tile in (tile_g, tile_s, tile_u):
                nc.gpsimd.memset(tile[:, :, 0:PAD], 0.0).then_inc(pads_set, 1)
            nc.gpsimd.memset(minus_half[:, :], -0.5).then_inc(pads_set, 1)
            nc.gpsimd.iota(inv_count[:, :], pattern=[[1, PAD]], base=1, channel_multiplier=0,
                           allow_small_or_imprecise_dtypes=True).then_inc(ranks_set, 1)
            nc.gpsimd.memset(ones[:, :], 1.0).then_inc(pads_set, 1)
            pool.wait_ge(pads_set, 5)
            nc.gpsimd.affine_select(out=ident[:, :], in_=ones[:, :], compare_op=ALU.is_equal, fill=0.0,
                                    base=0, pattern=[[1, P]], channel_multiplier=-1).then_inc(consts_set, 1)

            def add_squares(count, chunks=KD):
                for c in range(chunks):
                    pool.wait_ge(square_ready, count + c + 1)
                    if c == 0:
                        nc.gpsimd.sem_inc(squares_added, 1)
                        continue
                    pool.wait_ge(squares_added, count + c)
                    nc.gpsimd.tensor_tensor(square_sum[:, :], square_sum[:, :], body(tile_s, c % 2),
                                            ALU.add).then_inc(squares_added, 1)

            def root(norm):
                pool.wait_ge(mean_ready, norm + 1)
                nc.gpsimd.tensor_tensor(r_col[:, :], mean_col[:, :], minus_half[:, 0:TT],
                                        ALU.pow).then_inc(rcol_ready, 1)

            def silu(j, b):
                pool.wait_ge(sig_ready, j + 1)
                nc.gpsimd.tensor_tensor(body(tile_g, b), body(tile_g, b), body(tile_s, b),
                                        ALU.mult).then_inc(silu_ready, 1)

            def gate_up(f):
                u0, _, norm = ffn_count(f)
                root(norm)
                with pool.Fori(0, KF // 2) as i:
                    for j in range(2):
                        silu(u0 + j + 2 * i, j)

            def gelu(e):
                pool.wait_ge(gsig_ready, e + 1)
                if 2 <= e < TT:
                    pool.wait_ge(s_done, e - 1)
                arg = body(tile_g, e % 2) if e < TT else gelu_u(e - TT)
                out = body(tile_u, e % 2) if e < TT else arg
                nc.gpsimd.tensor_tensor(out, arg, body(tile_s, e % 2), ALU.mult).then_inc(gelu_ready, 1)

            add_squares(0)
            gate_up(0)
            add_squares(KD)
            root(1)
            p, j = PAIR_OF[MIX_GRAIN + MIX_S]
            pool.wait_ge(weights_loaded[p % 2], 16 * (p // 2 + 1))
            spatial = w_raw[:, SLOT_OF[MIX_GRAIN + MIX_S], :].rearrange("p (h t) -> p h t", t=P)
            nc.gpsimd.affine_select(out=spatial, in_=spatial, compare_op=ALU.is_ge, fill=0.0, base=0,
                                    pattern=[[0, A_HEADS], [1, P]], channel_multiplier=-1).then_inc(masked, 1)
            for pair in range(2):
                es = (2 * pair, 2 * pair + 1)
                for e in es:
                    gelu(e)
                for e in es:
                    pool.wait_ge(vmean_ready, e + 1)
                    nc.gpsimd.tensor_tensor(v_scale[:, e % 2, :], v_sums[:, e % 2, :], minus_half[:, :],
                                            ALU.pow).then_inc(vscale_ready, 1)
            for e in range(TT, 2 * TT):
                gelu(e)
            add_squares(2 * KD)
            gate_up(1)
            add_squares(3 * KD, KD - 2)
            root(3)


def kernel(**inputs):
    import numpy as np
    import concourse.bacc as bacc
    from concourse.bass_utils import run_bass_kernel_spmd

    a = {k: np.asarray(v) for k, v in inputs.items()}

    def by_rows(w, columns, k):
        return w.reshape(k, P, columns).transpose(1, 0, 2).reshape(P, k * columns)

    def ffn(tag):
        gate, up, down = (a[f"{tag}_w_{n}"][0] for n in ("gate", "up", "down"))
        grains = [by_rows(w[:, j * P:(j + 1) * P], P, KD) for j in range(KF) for w in (gate, up)]
        return grains + projection(down, range(QUAD_F))

    def projection(w, order):
        half = HALF * P
        return [by_rows(w[2 * g * P:2 * (g + 1) * P, q * half:(q + 1) * half], half, 2)
                for q in range(2) for g in order]

    w_in = a["w_in"][0]
    u_w, v_w, z_w = (w_in[:, n * A_WIDTH:(n + 1) * A_WIDTH] for n in range(3))
    tile = lambda w, i: by_rows(w[:, i * P:(i + 1) * P], P, KD)
    pool_w = np.zeros((P, GRAIN), np.float32)
    pool_w[:, 0:TT * P] = by_rows(a["pool_w"][0].reshape(4 * P, P), P, 4)
    spatial = a["gmlp_w_s"][0].transpose(2, 0, 1).reshape(P, GRAIN)
    grains = ffn("ffn1")
    grains += [tile(z_w, i) for i in range(4)]
    grains += [by_rows(v_w[2 * g * P:2 * (g + 1) * P], A_WIDTH, 2) for g in range(4)]
    grains += [pool_w] + [tile(u_w, i) for i in range(4)] + [spatial]
    grains += projection(a["w_out"][0], (2, 3, 0, 1))
    grains += ffn("ffn2")
    stream = np.zeros((len(PAIRS), P, PAIR * GRAIN), np.float32)
    for n, g in enumerate(grains):
        p, j = PAIR_OF[n]
        stream[p, :, j * GRAIN:(j + 1) * GRAIN] = g
    columns = np.concatenate([a[k].reshape(-1, P) for k in (
        "ffn1_norm", "ffn2_norm", "mix_norm", "final_norm", "gmlp_v_norm", "pool_scale")]).T
    bias = a["gmlp_b_s"][0].reshape(A_HEADS // 2, 2, P).transpose(1, 0, 2)
    arrays = {
        "in_x": np.ascontiguousarray(a["x"][0].T).reshape(KD, P, SEQ),
        "in_stream": stream,
        "in_columns": np.ascontiguousarray(columns),
        "in_bias": np.ascontiguousarray(bias),
    }
    nc = bacc.Bacc("TRN2", target_bir_lowering=False, num_devices=1)
    args = [nc.dram_tensor(name, v.shape, F32, kind="ExternalInput").ap() for name, v in arrays.items()]
    args.append(nc.dram_tensor("out_t", (KD, P, SEQ), F32, kind="ExternalOutput").ap())
    build_block(nc, *args)
    r = run_bass_kernel_spmd(nc, [arrays], core_ids=[0])
    return np.ascontiguousarray(r.results[0]["out_t"].reshape(D_MODEL, SEQ).T)[None]
```
